# Optimizing a Trainium2 kernel written in Bass

```python
import math
import jax, jax.numpy as jnp
from jax import lax
import numpy as np

D_MODEL = 1024
BATCH = 1
SEQ = 512
DEPTH = 1

HG_HEADS = 4
HG_KDIM = 128
HG_VDIM = 128
HG_WIDTH = HG_HEADS * HG_VDIM
HG_FDIM = HG_HEADS * HG_KDIM
HG_CHUNK = 64
ATT_HEADS = 4
ATT_HEAD_DIM = 128
ATT_WIDTH = ATT_HEADS * ATT_HEAD_DIM
IDX_HEADS = 8
IDX_DIM = 64
INDEX_TOPK_MAX = 256
QUERY_BLOCK = 128
D_MIX = HG_WIDTH + ATT_WIDTH
ROPE_THETA = 500000.0
ROPE_FRACTION = 4
D_FF = -(-8 * D_MODEL // (3 * 256)) * 256
N_MOD = 6
EPS = 1e-6

IN_SIZES = (HG_FDIM, HG_FDIM, HG_WIDTH, HG_WIDTH,
            ATT_WIDTH, ATT_WIDTH, ATT_WIDTH,
            IDX_HEADS * IDX_DIM, IDX_DIM, IDX_HEADS)
D_IN = sum(IN_SIZES)

kernel_name = "hymba_hgrn2_dsa_block"

def rmsnorm(x, gain):
    xf = x.astype(jnp.float32)
    y = xf * lax.rsqrt(jnp.mean(xf * xf, axis=-1, keepdims=True) + EPS)
    return (y * gain.astype(jnp.float32)).astype(x.dtype)

def layernorm(x, w, b):
    xf = x.astype(jnp.float32)
    mu = jnp.mean(xf, axis=-1, keepdims=True)
    var = jnp.mean(jnp.square(xf - mu), axis=-1, keepdims=True)
    y = (xf - mu) * lax.rsqrt(var + EPS)
    return (y * w.astype(jnp.float32) + b.astype(jnp.float32)).astype(x.dtype)

def partial_rope(x, positions):
    d = x.shape[-1]
    rot = d // ROPE_FRACTION
    half = rot // 2
    inv_freq = ROPE_THETA ** (-jnp.arange(half, dtype=jnp.float32) / half)
    ang = positions.astype(jnp.float32)[..., None] * inv_freq
    cos = jnp.cos(ang)[:, :, None, :]
    sin = jnp.sin(ang)[:, :, None, :]
    xf = x.astype(jnp.float32)
    x1, x2, xp = xf[..., :half], xf[..., half:rot], xf[..., rot:]
    out = jnp.concatenate([x1 * cos - x2 * sin, x2 * cos + x1 * sin, xp], axis=-1)
    return out.astype(x.dtype)

def hgrn2_mixer(q, f_raw, i, g_out, lower_bound, out_norm):
    B, T, _ = q.shape
    nc = T // HG_CHUNK
    dt = q.dtype
    qf = jax.nn.silu(q.astype(jnp.float32)) * HG_KDIM ** -0.5
    f = lower_bound + (1.0 - lower_bound) * jax.nn.sigmoid(f_raw.astype(jnp.float32))
    k = 1.0 - f
    logf = jnp.log(f)

    def chunks(a, d):
        return a.reshape(B, nc, HG_CHUNK, HG_HEADS, d).transpose(1, 0, 3, 2, 4)

    qc, kc = chunks(qf, HG_KDIM), chunks(k, HG_KDIM)
    gc = jnp.cumsum(chunks(logf, HG_KDIM), axis=3)
    vc = chunks(i.astype(jnp.float32), HG_VDIM)
    causal = jnp.tril(jnp.ones((HG_CHUNK, HG_CHUNK), dtype=bool))

    def step(S, inp):
        qb, kb, vb, gb = inp
        o_inter = jnp.einsum('bhtk,bhkv->bhtv', qb * jnp.exp(gb), S)
        diff = gb[:, :, :, None, :] - gb[:, :, None, :, :]
        decay = jnp.exp(jnp.where(causal[None, None, :, :, None], diff, -jnp.inf))
        A = jnp.einsum('bhtk,bhsk,bhtsk->bhts', qb, kb, decay)
        o_intra = jnp.einsum('bhts,bhsv->bhtv', A, vb)
        g_last = gb[:, :, -1]
        S_new = jnp.exp(g_last)[..., None] * S + jnp.einsum(
            'bhsk,bhsv->bhkv', kb * jnp.exp(g_last[:, :, None, :] - gb), vb)
        return S_new, o_inter + o_intra

    S0 = jnp.zeros((B, HG_HEADS, HG_KDIM, HG_VDIM), jnp.float32)
    _, o = lax.scan(step, S0, (qc, kc, vc, gc))
    o = o.transpose(1, 0, 3, 2, 4).reshape(B, T, HG_HEADS, HG_VDIM)
    o = o * lax.rsqrt(jnp.mean(o * o, axis=-1, keepdims=True) + EPS)
    o = o * out_norm.astype(jnp.float32).reshape(HG_HEADS, HG_VDIM)
    o = o.reshape(B, T, HG_WIDTH) * jax.nn.silu(g_out.astype(jnp.float32))
    return o.astype(dt)

def dsa_mixer(q, k, v, q_idx, k_idx, w_idx, positions, k_norm_w, k_norm_b):
    B, T, _ = q.shape
    topk = min(INDEX_TOPK_MAX, T // 4)
    nb = T // QUERY_BLOCK
    q = partial_rope(q.reshape(B, T, ATT_HEADS, ATT_HEAD_DIM), positions)
    k = partial_rope(k.reshape(B, T, ATT_HEADS, ATT_HEAD_DIM), positions)
    v = v.reshape(B, T, ATT_HEADS, ATT_HEAD_DIM)
    q_idx = partial_rope(q_idx.reshape(B, T, IDX_HEADS, IDX_DIM), positions)
    k_idx = layernorm(k_idx, k_norm_w, k_norm_b)
    k_idx = partial_rope(k_idx[:, :, None, :], positions)[:, :, 0, :]
    w_idx = w_idx * (IDX_HEADS ** -0.5 * IDX_DIM ** -0.5)
    key_pos = jnp.arange(T, dtype=jnp.int32)
    gather = jax.vmap(lambda a, ix: a[ix])
    scale = ATT_HEAD_DIM ** -0.5

    def to_blocks(a):
        return a.reshape(B, nb, QUERY_BLOCK, *a.shape[2:]).swapaxes(0, 1)

    def block(args):
        qi, wi, qb, tq = args
        s = jnp.einsum('bqhd,bsd->bqhs', qi, k_idx)
        score = jnp.einsum('bqh,bqhs->bqs', wi, jax.nn.relu(s)).astype(jnp.float32)
        score = jnp.where(key_pos[None, None, :] <= tq[None, :, None], score, -jnp.inf)
        _, idx = lax.top_k(score, topk)
        valid = idx <= tq[None, :, None]
        ks = gather(k, idx)
        vs = gather(v, idx)
        logits = jnp.einsum('bqhd,bqkhd->bhqk', qb, ks).astype(jnp.float32) * scale
        logits = jnp.where(valid[:, None], logits, -jnp.inf)
        p = jax.nn.softmax(logits, axis=-1).astype(vs.dtype)
        return jnp.einsum('bhqk,bqkhd->bqhd', p, vs)

    o = lax.map(block, (to_blocks(q_idx), to_blocks(w_idx), to_blocks(q),
                        key_pos.reshape(nb, QUERY_BLOCK)))
    return o.swapaxes(0, 1).reshape(B, T, ATT_WIDTH)

def setup_inputs(seed: int = 0) -> dict:
    key = jax.random.key(seed)
    ks = jax.random.split(key, 20)
    nrm = lambda k, shape, s: jax.random.normal(k, shape, jnp.float32) * s
    gain = lambda k, shape: 1.0 + 0.02 * jax.random.normal(k, shape, jnp.float32)
    x = nrm(ks[0], (BATCH, SEQ, D_MODEL), 1.0)
    c = nrm(ks[1], (BATCH, D_MODEL), 1.0)
    positions = (jnp.arange(SEQ, dtype=jnp.int32)[None, :]
                 + jax.random.randint(ks[2], (BATCH, 1), 0, 4096, dtype=jnp.int32))
    return {
        "x": x,
        "c": c,
        "positions": positions,
        "w_ada": nrm(ks[3], (DEPTH, D_MODEL, N_MOD * D_MODEL), 0.5 * D_MODEL ** -0.5),
        "b_ada": nrm(ks[4], (DEPTH, N_MOD * D_MODEL), 0.01),
        "norm_pre_mix": gain(ks[5], (DEPTH, D_MODEL)),
        "norm_post_mix": gain(ks[6], (DEPTH, D_MODEL)),
        "norm_pre_ffn": gain(ks[7], (DEPTH, D_MODEL)),
        "norm_post_ffn": gain(ks[8], (DEPTH, D_MODEL)),
        "w_in": nrm(ks[9], (DEPTH, D_MODEL, D_IN), D_MODEL ** -0.5),
        "hgrn_lower_bound": nrm(ks[10], (DEPTH + 1, HG_FDIM), 1.0),
        "hgrn_out_norm": gain(ks[11], (DEPTH, HG_WIDTH)),
        "idx_k_norm_w": gain(ks[12], (DEPTH, IDX_DIM)),
        "idx_k_norm_b": nrm(ks[13], (DEPTH, IDX_DIM), 0.02),
        "w_out": nrm(ks[14], (DEPTH, D_MIX, D_MODEL), D_MIX ** -0.5),
        "w_ffn_in": nrm(ks[15], (DEPTH, D_MODEL, 2 * D_FF), D_MODEL ** -0.5),
        "w_ffn_out": nrm(ks[16], (DEPTH, D_FF, D_MODEL), D_FF ** -0.5),
    }

def reference(x, c, positions, w_ada, b_ada, norm_pre_mix, norm_post_mix, norm_pre_ffn,
              norm_post_ffn, w_in, hgrn_lower_bound, hgrn_out_norm, idx_k_norm_w, idx_k_norm_b,
              w_out, w_ffn_in, w_ffn_out):
    split_points = np.cumsum(IN_SIZES)[:-1].tolist()
    lb_all = jnp.cumsum(jax.nn.softmax(hgrn_lower_bound.astype(jnp.float32), axis=0), axis=0)
    for layer in range(DEPTH):
        mod = jax.nn.silu(c) @ w_ada[layer] + b_ada[layer]
        sh_m, sc_m, gt_m, sh_f, sc_f, gt_f = [m[:, None, :] for m in jnp.split(mod, N_MOD, axis=-1)]

        h = rmsnorm(x, norm_pre_mix[layer]) * (1.0 + sc_m) + sh_m
        proj = h @ w_in[layer]
        (hq, hf, hi, hg, aq, ak, av, iq, ik, iw) = jnp.split(proj, split_points, axis=-1)
        o_hg = hgrn2_mixer(hq, hf, hi, hg, lb_all[layer], hgrn_out_norm[layer])
        o_att = dsa_mixer(aq, ak, av, iq, ik, iw, positions,
                          idx_k_norm_w[layer], idx_k_norm_b[layer])
        y = jnp.concatenate([o_hg, o_att], axis=-1) @ w_out[layer]
        x = x + gt_m * rmsnorm(y, norm_post_mix[layer])

        h = rmsnorm(x, norm_pre_ffn[layer]) * (1.0 + sc_f) + sh_f
        gate, up = jnp.split(h @ w_ffn_in[layer], 2, axis=-1)
        y = (jax.nn.silu(gate) * up) @ w_ffn_out[layer]
        x = x + gt_f * rmsnorm(y, norm_post_ffn[layer])
    return x


_drawn_inputs = setup_inputs


def setup_inputs(seed=0):
    import zlib

    import numpy as np

    out = dict(_drawn_inputs(seed))
    spreads = {}
    factors = {'b_ada': 3.092,
     'norm_pre_mix': 4.832,
     'norm_post_mix': 8.0,
     'norm_pre_ffn': 22.583,
     'norm_post_ffn': 35.699,
     'hgrn_out_norm': 8.0,
     'idx_k_norm_w': 8.0,
     'idx_k_norm_b': 8.0}
    for name, (base, spread) in spreads.items():
        noise = np.random.default_rng([zlib.crc32(name.encode()), seed]).standard_normal(out[name].shape)
        drawn = base * np.exp(spread * noise) if base else spread * noise
        out[name] = __import__('jax').numpy.asarray(drawn.astype(out[name].dtype))
    for name, factor in factors.items():
        out[name] = (out[name] * factor).astype(out[name].dtype)
    return out
```

```python
from contextlib import ExitStack

import numpy as np

import concourse.bass as bass
from concourse import mybir

P = 128
D_MODEL = 1024
SEQ = 512
HG_HEADS = 4
ATT_HEADS = 4
HEAD = 128
IDX_HEADS = 8
IDX_DIM = 64
TOPK = min(256, SEQ // 4)
D_FF = -(-8 * D_MODEL // (3 * 256)) * 256
ROPE_THETA = 500000.0
EPS = 1e-6
KT = D_MODEL // P
TT = SEQ // P
FT = D_FF // P
COL_Q, COL_F, COL_I, COL_G = 0, 512, 1024, 1536
COL_AQ, COL_AK, COL_AV, COL_IQ, COL_IK = 2048, 2560, 3072, 3584, 4096
IK_COLS = IDX_DIM + IDX_HEADS
D_IN = COL_IK + IK_COLS

G_IDX, G_HG, G_ATT, G_OUT, G_FIN, G_FOUT = 0, 5, 21, 33, 41, 85
N_GROUPS = G_FOUT + FT
U_HG, U_ATT, U_OUT, U_FIN, U_FOUT = (1, 1, 1, 2), (5, 5, 5), (9, 9, 9, 6), (11, 11, 11, 8), (22, 22, 22, 19)
ADA_ON_VE, ADA_ON_POOL = (6, 8, 10, 12, 14, 15), (5, 7, 9, 11, 13)
START_ADA = 16
LEVELS = 10
ROUNDS = TOPK // 8
NEG = -1e30
TAKEN = -3e38

C_BADA, C_C, C_PRE_MIX, C_POST_MIX, C_PRE_FFN, C_POST_FFN, C_ONORM, C_LB = 0, 48, 56, 64, 72, 80, 88, 92
N_PRM = 100


def build(nc, x, c, positions, w_ada, b_ada, norm_pre_mix, norm_post_mix, norm_pre_ffn, norm_post_ffn, w_in,
          hgrn_lower_bound, hgrn_out_norm, idx_k_norm_w, idx_k_norm_b, w_out, w_ffn_in, w_ffn_out, rope_const, out):
    f32, f32r, u32, i32 = mybir.dt.float32, mybir.dt.float32r, mybir.dt.uint32, mybir.dt.int32
    ALU, ACT = mybir.AluOpType, mybir.ActivationFunctionType
    ds = bass.ds
    ctx = ExitStack()
    with ctx:
        def sb(name, cols, dt=f32, parts=P):
            return ctx.enter_context(nc.sbuf_tensor(name, [parts, cols], dt))

        def sem(name):
            return ctx.enter_context(nc.semaphore(name))

        h_hi, h_lo = sb("h_hi", KT * SEQ, f32r), sb("h_lo", KT * SEQ, f32r)
        w_raw = [sb(f"w_raw{s}", 1024) for s in range(4)]
        w_hi = [sb(f"w_hi{s}", 1024, f32r) for s in range(4)]
        w_lo = [sb(f"w_lo{s}", 1024, f32r) for s in range(4)]
        mix = sb("mix", KT * SEQ)
        act = sb("act", FT * SEQ)
        res = sb("res", 5376)
        score = sb("score", 1152)
        bias = sb("bias", 1280)
        rope = sb("rope", 2048)
        adaw = [sb(f"adaw{s}", 1024) for s in range(2)]
        ada_part = sb("ada_part", 4 * P)
        gate_ffn = sb("gate_ffn", D_MODEL)
        masks = sb("masks", 7 * P)
        ident = sb("ident", P)
        ones = sb("ones", P)
        dup = sb("dup", P)
        swap_head = sb("swap_head", 32, parts=32)
        swap_idx = sb("swap_idx", P)
        prm_rows = sb("prm_rows", P)
        prm = sb("prm", N_PRM)
        rc = sb("rc", 4)
        knorm = sb("knorm", 2)
        silu_c = sb("silu_c", KT)
        mod = sb("mod", 48)
        scale_mix, scale_ffn = sb("scale_mix", KT), sb("scale_ffn", KT)
        gate_cols = sb("gate_cols", 2 * KT)
        hg_par = sb("hg_par", 3 * HG_HEADS)
        hp = sb("hp", 3)
        lb_diff = sb("lb_diff", HG_HEADS)
        eps = sb("eps", 1)
        w_tok = sb("w_tok", IDX_HEADS * TT)
        ss, rstd = sb("ss", 16), sb("rstd", 8)
        top8 = sb("top8", 24)
        mx, nmx, rs, ri = sb("mx", TT), sb("nmx", TT), sb("rs", TT), sb("ri", TT)

        def part(t, at, n=SEQ):
            return t[:, at:at + n]

        f_, q_sig, q_raw, g_sig, g_raw, q_f, k_b, tot, i_t, i_tok, o_sq, o_rstd, o_n = (
            part(act, n * SEQ) for n in range(13))
        att_hg = act[:, 13 * SEQ:13 * SEQ + 2560]
        at_diag = att_hg.rearrange("p (c x) -> p c x", x=SEQ + P)[:, :, 0:P]
        xn = part(act, 0, TT * D_MODEL)
        h32 = [part(act, n) for n in (4096, 4608, 9728, 10752)]
        junk = part(act, 5120, 1024)
        y_tmp = [part(act, 6144), part(act, 6656)]
        diag = part(act, 0, 2048)
        ang = [part(act, 7168 + SEQ * n) for n in range(4)]
        pos_i = part(act, 9216)
        pos, turn_fix = part(act, 5120), part(act, 5632)
        f_w, g_w = part(act, 9216), part(act, 9728)
        xr = part(res, 0, TT * D_MODEL)
        iq = part(res, 0, 2048)
        ik, ikw, r_tmp = part(res, 2048), part(res, 2560), part(res, 3072)
        relu = [part(res, 3584), part(res, 4096)]
        r_tmp2 = part(res, 4608)
        pt = part(res, 0, 2048)
        aq, ak, av, av_tok = part(res, 2048), part(res, 2560), part(res, 3072), part(res, 3584)
        p_off = [4096, 4224, 4480, 4864]
        probs = [part(res, p_off[t], P * (t + 1)) for t in range(TT)]
        gate_mix = part(score, 0, 1024)
        s_off = [None, 0, 256, 640]
        b_off = [0, 128, 384, 768]
        sc_t = [None] + [part(score, s_off[t], P * (t + 1)) for t in range(1, TT)]
        bias_t = [part(bias, b_off[t], P * (t + 1)) for t in range(TT)]
        cos_h, sin_h, cos_i, sin_i = (part(rope, n * SEQ) for n in range(4))
        silu_g = [part(adaw[0], 0), part(adaw[0], SEQ)]
        start_slot = ([part(mix, n * 1024, 1024) for n in range(4)] +
                      [part(t, at, 1024) for t, at in ((adaw[0], 0), (adaw[1], 0), (act, 9728), (score, 0), (bias, P),
                                                       (res, 4096), (act, 6144), (gate_ffn, 0))])

        ps = [ctx.enter_context(nc.psum_tensor(f"ps{b}", [P, SEQ], f32)) for b in range(8)]

        const_step, consts = sem("const_step"), sem("consts")
        prm_loaded, pos_loaded = sem("prm_loaded"), sem("pos_loaded")
        x_loaded = [sem(f"x_loaded{t}") for t in range(TT)]
        start_loaded = [sem(f"start_loaded{n}") for n in range(START_ADA)]
        x_again = sem("x_again")
        prm_mm, prm_ok, silu_ok, lbd_ok, lb_ok = sem("prm_mm"), sem("prm_ok"), sem("silu_ok"), sem("lbd_ok"), sem("lb_ok")
        small = sem("small")
        ada_loaded = [sem(f"ada_loaded{s}") for s in range(2)]
        ada_used, mod_ok, scale_ok = sem("ada_used"), sem("mod_ok"), sem("scale_ok")
        ada_step, ada_sum = sem("ada_step"), sem("ada_sum")
        ada_start, ada_first, ada_late = sem("ada_start"), sem("ada_first"), sem("ada_late")
        w_loaded = [sem(f"w_loaded{s}") for s in range(4)]
        hi_ok, lo_ok, group_done = sem("hi_ok"), sem("lo_ok"), sem("group_done")
        acc_free = [sem(f"acc_free{b}") for b in range(2)]
        ang_step, sin_ok = sem("ang_step"), sem("sin_ok")
        ss_ok, ln_ok, rstd_ok, xn_ok = sem("ss_ok"), sem("ln_ok"), sem("rstd_ok"), sem("xn_ok")
        xt_mm, h32_even, h32_odd, hhi_ok, hlo_ok = (sem(n) for n in ("xt_mm", "h32_even", "h32_odd", "hhi_ok", "hlo_ok"))
        idx_raw, idx_swap, idx_t, idx_ok = sem("idx_raw"), sem("idx_swap"), sem("idx_t"), sem("idx_ok")
        ikm_mm, ikc_ok, iksq_ok, ikv_mm, ikln, ikr_ok = (sem(n) for n in (
            "ikm_mm", "ikc_ok", "iksq_ok", "ikv_mm", "ikln", "ikr_ok"))
        ikn_step, ikn_ok, ikd_mm, ik_ok, wt_mm, wt_ok = (sem(n) for n in (
            "ikn_step", "ikn_ok", "ikd_mm", "ik_ok", "wt_mm", "wt_ok"))
        sc_mm, sc_relu, sc_acc, causal_ok = sem("sc_mm"), sem("sc_relu"), sem("sc_acc"), sem("causal_ok")
        top_max, top_rep, bias_ok = sem("top_max"), sem("top_rep"), sem("bias_ok")
        f_sig, f_ok, hp_ok, q_ok, i_raw, iv_mm, iv_ok, g_ok = (sem(n) for n in (
            "f_sig", "f_ok", "hp_ok", "q_ok", "i_raw", "iv_mm", "iv_ok", "g_ok"))
        lvl_ready, lvl_mm, lvl_out, tot_ok = sem("lvl_ready"), sem("lvl_mm"), sem("lvl_out"), sem("tot_ok")
        o_mm, osq_ok, oss_mm, oln_ok, ors_ok, on_ok, hg_out = (sem(n) for n in (
            "o_mm", "osq_ok", "oss_mm", "oln_ok", "ors_ok", "on_ok", "hg_out"))
        a_raw, a_swap, a_t, a_rope, v_mm, v_ok = (sem(n) for n in ("a_raw", "a_swap", "a_t", "a_rope", "v_mm", "v_ok"))
        lg_mm, lg_ok, nm_ok, exp_ok, ri_ok, p_ok, pt_mm, pt_ok, pv_mm, att_out = (sem(n) for n in (
            "lg_mm", "lg_ok", "nm_ok", "exp_ok", "ri_ok", "p_ok", "pt_mm", "pt_ok", "pv_mm", "att_out"))
        raw_taken, tile_done, yb_ok = sem("raw_taken"), sem("tile_done"), sem("yb_ok")
        gc_ok, diag_ok, gate_mm, gate_ok = sem("gc_ok"), sem("diag_ok"), sem("gate_mm"), sem("gate_ok")
        xs_hi, xs_ok = sem("xs_hi"), sem("xs_ok")
        ysq_ok, yln_ok, yrs_ok, yt_ok, res_ok = (sem(n) for n in ("ysq_ok", "yln_ok", "yrs_ok", "yt_ok", "res_ok"))
        silu_done, act_ok = [sem(f"silu_done{v}") for v in range(2)], [sem(f"act_ok{v}") for v in range(2)]
        stored = sem("stored")
        sp_waits, po_waits, ve_waits, te_waits = sem("sp_waits"), sem("po_waits"), sem("ve_waits"), sem("te_waits")

        block = ctx.enter_context(nc.Block())

        def idx_slot(n):
            return (n + 3) % 4, (1 if n == 4 else 0)

        @block.sync
        def _(sp):
            def wait_apart(s, value):
                sp.wait_ge(s, value)
                sp.sem_inc(sp_waits, 1)

            for t in range(TT):
                sp.dma_start(xr[:, t * D_MODEL:(t + 1) * D_MODEL], x[0, t * P:(t + 1) * P, :]).then_inc(x_loaded[t], 16)

            def ada_cols(col):
                return w_ada[0].rearrange("(k p) n -> p k n", p=P)[:, :, ds(col * P, P)]

            for n in range(START_ADA):
                if n >= len(start_slot):
                    sp.wait_ge(ada_used, n - len(start_slot) + 1)
                sp.dma_start(start_slot[n % len(start_slot)].rearrange("p (k n) -> p k n", k=KT), ada_cols(n)).then_inc(start_loaded[n], 16)

            def load_cols(src, col, n, slot):
                sp.dma_start(w_raw[slot][:, 0:KT * n].rearrange("p (k n) -> p k n", k=KT),
                             src[0].rearrange("(k p) n -> p k n", p=P)[:, :, ds(col, n)]).then_inc(w_loaded[slot], 16)

            def load_rows(src, k, slot):
                sp.dma_start(w_raw[slot][:, :], src[0][ds(k * P, P), :]).then_inc(w_loaded[slot], 16)

            for n in range(4):
                load_cols(w_in, COL_IQ + n * P, P, idx_slot(n)[0])
            sp.wait_ge(lo_ok, 1)
            load_cols(w_in, COL_IK, IK_COLS, 3)
            hg_cols = (COL_F, COL_Q, COL_I, COL_G)

            def load_hg(h, j):
                wait_apart(lo_ok, h * 4 + (j + 2))
                load_cols(w_in, h * P + hg_cols[j], P, j)

            def load_att(h, j):
                wait_apart(lo_ok, h * 3 + (19 + j))
                load_cols(w_in, h * P + (COL_AQ, COL_AK, COL_AV)[j], P, j)

            def load_out(k, free):
                wait_apart(lo_ok, free)
                load_rows(w_out, k, k % 4)

            def load_ada(col, c):
                sp.dma_start(adaw[c % 2][:, :].rearrange("p (k n) -> p k n", k=KT),
                             ada_cols(col)).then_inc(ada_loaded[c % 2], 16)

            def load_gates_ada(s, c):
                if isinstance(s, int) and s == 0 and c < 2:
                    sp.wait_ge(ada_used, START_ADA)
                else:
                    wait_apart(ada_step, s * 16 + (4 * c - 4))
                load_ada(s * 2 + ((16, 17, 40, 41)[c]), c)

            def load_norm_ada(h, pair):
                if isinstance(h, int) and h == 0 and pair == 0:
                    sp.wait_ge(ada_step, 16 * HG_HEADS)
                else:
                    wait_apart(ada_late, h * 32 + 16 * pair)
                for c in range(2):
                    load_ada(h * 4 + (24 + 2 * pair + c), c)

            for j in range(4):
                load_hg(0, j)
            for c in range(2):
                load_gates_ada(0, c)
            load_hg(1, 0)
            load_hg(1, 1)
            with sp.Fori(0, 2) as s:
                load_hg(s + 1, 2)
                load_gates_ada(s, 2)
                load_hg(s + 1, 3)
                load_gates_ada(s, 3)
                load_hg(s + 2, 0)
                load_gates_ada(s + 1, 0)
                load_hg(s + 2, 1)
                load_gates_ada(s + 1, 1)
            load_hg(3, 2)
            load_gates_ada(2, 2)
            load_hg(3, 3)
            load_gates_ada(2, 3)
            load_att(0, 0)
            load_gates_ada(3, 0)
            load_att(0, 1)
            load_gates_ada(3, 1)
            load_att(0, 2)
            load_gates_ada(3, 2)
            load_gates_ada(3, 3)
            load_att(1, 0)
            load_att(1, 1)
            load_norm_ada(0, 0)
            with sp.Fori(0, 2) as h:
                load_att(h + 1, 2)
                load_norm_ada(h, 1)
                load_norm_ada(h + 1, 0)
                load_att(h + 2, 0)
                load_att(h + 2, 1)
            load_att(3, 2)
            load_norm_ada(2, 1)
            load_norm_ada(3, 0)
            load_out(0, 31)
            load_out(1, 32)
            load_out(2, 33)
            load_out(3, 33)
            load_norm_ada(3, 1)
            load_out(4, 34)
            for k in range(5, KT):
                load_out(k, 30 + k)
            sp.wait_ge(att_out, ATT_HEADS)
            for t in range(TT):
                sp.dma_start(xr[:, t * D_MODEL:(t + 1) * D_MODEL], x[0, t * P:(t + 1) * P, :]).then_inc(x_again, 16)
            with sp.Fori(0, FT // 2) as i:
                for u, (tile, half) in enumerate(((0, 0), (0, 1), (1, 0), (1, 1))):
                    wait_apart(lo_ok, i * 4 + (G_FIN - 3 + u))
                    load_cols(w_ffn_in, i * 256 + (half * D_FF + tile * P), P, u)
            with sp.Fori(0, FT // 4) as i:
                for u in range(4):
                    wait_apart(lo_ok, i * 4 + (G_FOUT - 3 + u))
                    load_rows(w_ffn_out, i * 4 + u, u)
            for k in range(FT // 4 * 4, FT):
                sp.wait_ge(lo_ok, G_FOUT - 3 + k)
                load_rows(w_ffn_out, k, k % 4)
            for t in range(TT):
                sp.wait_ge(res_ok, 8 + 2 * (t + 1))
                sp.dma_start(out[0, t * P:(t + 1) * P, :], xr[:, t * D_MODEL:(t + 1) * D_MODEL]).then_inc(stored, 16)
            sp.wait_ge(stored, 16 * TT)

        @block.gpsimd
        def _(pool):
            steps = [0]

            def step(ins):
                steps[0] += 1
                ins.then_inc(const_step, 1)
                pool.wait_ge(const_step, steps[0])

            step(pool.memset(ones[:, :], 1.0))
            step(pool.memset(eps[:, :], EPS))
            step(pool.affine_select(out=ident[:, :], in_=ones[:, :], compare_op=ALU.is_equal, fill=0.0, base=0,
                                    pattern=[[-1, P]], channel_multiplier=1))
            for half in range(2):
                step(pool.tensor_copy(dup[0:IDX_DIM, half * IDX_DIM:(half + 1) * IDX_DIM],
                                      ident[0:IDX_DIM, 0:IDX_DIM]))
            step(pool.memset(swap_head[:, :], 0.0))
            for lo in range(2):
                step(pool.affine_select(out=swap_head[:, 16 * lo:16 * lo + 16], in_=swap_head[:, 16 * lo:16 * lo + 16],
                                        compare_op=ALU.not_equal, fill=1.0, base=0 if lo else -16,
                                        pattern=[[-1, 16]], channel_multiplier=1))
            step(pool.memset(swap_idx[:, :], 0.0))
            for lo in range(2):
                v = swap_idx[:, :].rearrange("p (b n) -> p b n", b=2)[:, :, 8 * lo:8 * lo + 8]
                step(pool.affine_select(out=v, in_=v, compare_op=ALU.not_equal, fill=1.0, base=0 if lo else -8,
                                        pattern=[[-IDX_DIM, 2], [-1, 8]], channel_multiplier=1))
            step(pool.memset(bias_t[0], 0.0))
            step(pool.affine_select(out=bias_t[0], in_=bias_t[0], compare_op=ALU.is_ge, fill=NEG, base=0,
                                    pattern=[[-1, P]], channel_multiplier=1))
            for n in range(7):
                h, nb = 1 << n, P >> (n + 1)
                m = masks[:, n * P:(n + 1) * P]
                v = m.rearrange("p (b two h) -> p b two h", b=nb, two=2)
                step(pool.memset(m, 1.0))
                step(pool.memset(v[:, :, 0, :], 0.0))
                step(pool.affine_select(out=m, in_=m, compare_op=ALU.is_ge, fill=0.0, base=0,
                                        pattern=[[-2 * h, nb], [0, 2 * h]], channel_multiplier=1))
                step(pool.affine_select(out=m, in_=m, compare_op=ALU.is_ge, fill=0.0, base=h - 1,
                                        pattern=[[2 * h, nb], [0, 2 * h]], channel_multiplier=-1))
            pool.memset(top8[:, :], 0.0).then_inc(consts, 1)

            def split_lo(g, slot, n=1024):
                pool.wait_ge(hi_ok, g + 1)
                pool.tensor_tensor(w_lo[slot][:, 0:n], w_raw[slot][:, 0:n], w_hi[slot][:, 0:n].bitcast(f32),
                                   ALU.subtract).then_inc(lo_ok, 1)

            def wait_apart(s, value):
                pool.wait_ge(s, value)
                pool.sem_inc(po_waits, 1)

            def ada_column(s, c):
                wait_apart(ada_loaded[c % 2], s * 32 + (c // 2 * 16 + 16))
                if c == 0 and not (isinstance(s, int) and s == 0):
                    wait_apart(ada_sum, s)
                ada_product(adaw[c % 2], ada_part[:, c * P:(c + 1) * P], ada_step, s * 16 + 4 * c)

            def ada_product(w, dst, counter, done):
                pool.tensor_tensor(w[:, :].rearrange("p (k n) -> p k n", k=KT), w[:, :].rearrange("p (k n) -> p k n", k=KT),
                                   silu_c[:, :, None].to_broadcast([P, KT, P]), ALU.mult).then_inc(counter, 1)
                for n, half in enumerate((4 * P, 2 * P, P)):
                    wait_apart(counter, done + (n + 1))
                    pool.tensor_tensor(dst if half == P else w[:, 0:half], w[:, 0:half], w[:, half:2 * half],
                                       ALU.add).then_inc(counter, 1)

            pool.wait_ge(silu_ok, 1)
            for n, c in enumerate(ADA_ON_POOL):
                pool.wait_ge(start_loaded[c], 16)
                w = start_slot[c % len(start_slot)]
                ada_product(w, w[:, 0:P], ada_first, 4 * n)

            for n in range(5):
                split_lo(n, idx_slot(n)[0], KT * IK_COLS if n == 4 else 1024)
            split_lo(G_HG, 0)
            split_lo(G_HG + 1, 1)

            def stage_hg(h):
                for j, slot in enumerate((2, 3, 0, 1)):
                    split_lo(h * 4 + (G_HG + 2 + j), slot)
                    ada_column(h, j)

            def stage_att(h):
                for j, slot in enumerate((2, 0, 1)):
                    split_lo(h * 3 + (G_ATT + 2 + j), slot)

            stage_hg(0)
            with pool.Fori(1, HG_HEADS) as h:
                stage_hg(h)
            with pool.Fori(0, ATT_HEADS) as h:
                stage_att(h)

            def split_x_lo(k):
                pool.wait_ge(xs_hi, k + 1)
                part_k = slice(k * SEQ, (k + 1) * SEQ)
                pool.tensor_tensor(h_lo[:, part_k], mix[:, part_k], h_hi[:, part_k].bitcast(f32),
                                   ALU.subtract).then_inc(xs_ok, 1)

            split_lo(G_OUT + 2, 2)
            split_lo(G_OUT + 3, 3)
            for k in range(KT):
                split_x_lo(k)
            for k in range(4, KT):
                split_lo(G_OUT + k, k % 4)
            with pool.Fori(0, FT // 2) as i:
                for u in range(4):
                    split_lo(i * 4 + (G_FIN + u), u)
            with pool.Fori(0, FT // 4) as i:
                for u in range(4):
                    split_lo(i * 4 + (G_FOUT + u), u)
            for k in range(FT // 4 * 4, FT):
                split_lo(G_FOUT + k, k % 4)

        @block.scalar
        def _(sc):
            def split_hi(slot, use, free, n=1024):
                sc.wait_ge(w_loaded[slot], use * 16 + 16)
                if free is not None:
                    sc.wait_ge(group_done, free)
                sc.activation(w_hi[slot][:, 0:n], w_raw[slot][:, 0:n], ACT.Copy).then_inc(hi_ok, 1)

            rows = [(C_BADA, b_ada, 48), (C_C, c, 8), (C_PRE_MIX, norm_pre_mix, 8), (C_POST_MIX, norm_post_mix, 8),
                    (C_PRE_FFN, norm_pre_ffn, 8), (C_POST_FFN, norm_post_ffn, 8), (C_ONORM, hgrn_out_norm, 4)]
            for at, src, n in rows:
                sc.dma_start(prm_rows[at:at + n, :], src.rearrange("o (n p) -> (o n) p", p=P)).then_inc(prm_loaded, 16)
            sc.dma_start(prm_rows[C_LB:C_LB + 8, :],
                         hgrn_lower_bound.rearrange("o (n p) -> (o n) p", p=P)).then_inc(prm_loaded, 16)
            sc.dma_start(pos_i[:, :].bitcast(i32), positions.broadcast_to([P, SEQ])).then_inc(pos_loaded, 16)
            sc.dma_start(rc[:, :], rope_const).then_inc(pos_loaded, 16)
            sc.dma_start(knorm[0:IDX_DIM, 0:1], idx_k_norm_w.rearrange("o p -> p o")).then_inc(pos_loaded, 16)
            sc.dma_start(knorm[0:IDX_DIM, 1:2], idx_k_norm_b.rearrange("o p -> p o")).then_inc(pos_loaded, 16)
            sc.wait_ge(lbd_ok, 1)
            sc.activation(hg_par[:, :].rearrange("p (h n) -> p h n", n=3)[:, :, 1], lb_diff[:, :],
                          ACT.Sigmoid).then_inc(lb_ok, 1)
            sc.activation(silu_c[:, :], prm[:, C_C:C_C + KT], ACT.Silu).then_inc(silu_ok, 1)

            def row_stats(seen, t):
                n = TT * seen + t
                if seen:
                    sc.wait_ge(res_ok, 2 * (t + 1))
                    sc.wait_ge(ysq_ok, 2 * min(t + 2, TT))
                else:
                    sc.wait_ge(x_loaded[t], 16)
                if n:
                    sc.wait_ge(ss_ok, n)
                sc.activation(junk, xr[:, t * D_MODEL:(t + 1) * D_MODEL], ACT.Square,
                              accum_out=ss[:, t:t + 1]).then_inc(ss_ok, 1)
                sc.wait_ge(ss_ok, n + 1)
                sc.activation(rstd[:, t:t + 1], ss[:, t:t + 1], ACT.Ln, scale=1.0 / D_MODEL,
                              bias=eps[:, :]).then_inc(ln_ok, 1)
                sc.wait_ge(ln_ok, n + 1)
                sc.activation(rstd[:, t:t + 1], rstd[:, t:t + 1], ACT.Exp, scale=-0.5).then_inc(rstd_ok, 1)

            def norm_hi(seen, shift_at, scale_cols):
                for k in range(0, KT, 2):
                    n = KT * seen + k
                    sc.wait_ge(xt_mm, n + 2)
                    if k >= 4:
                        sc.wait_ge(hlo_ok, n - 2)
                    sc.activation(h32[(k + 1) % 4], ps[k + 1][:, :], ACT.Identity, scale=scale_cols[:, k + 1:k + 2],
                                  bias=mod[:, shift_at + k + 1:shift_at + k + 2]).then_inc(h32_odd, 1)
                    sc.wait_ge(h32_even, n // 2 + 1)
                    sc.activation(h_hi[:, k * SEQ:(k + 1) * SEQ], h32[k % 4], ACT.Copy).then_inc(hhi_ok, 1)
                    sc.wait_ge(h32_odd, n // 2 + 1)
                    sc.activation(h_hi[:, (k + 1) * SEQ:(k + 2) * SEQ], h32[(k + 1) % 4], ACT.Copy).then_inc(hhi_ok, 1)

            nc.scalar.preload_act_table_set("natural_log_exp_and_others")
            sc.wait_ge(const_step, 2)
            for t in range(TT):
                row_stats(0, t)
            def sines(n):
                sc.wait_ge(ang_step, (12, 14, 25, 27)[n])
                sc.activation((cos_i, sin_i, cos_h, sin_h)[n], ang[(2, 3, 0, 1)[n]], ACT.Sin).then_inc(sin_ok, 1)

            split_hi(3, 0, None)
            split_hi(0, 0, None)
            sc.wait_ge(scale_ok, 1)
            norm_hi(0, 0, scale_mix)

            for n in range(5):
                rows = IK_COLS if n == 4 else P
                sc.wait_ge(group_done, n + 1)
                sc.activation(ikw[0:rows, :] if n == 4 else iq[:, n * SEQ:(n + 1) * SEQ], ps[n % 2][0:rows, :],
                              ACT.Copy).then_inc(acc_free[n % 2], 1)
                if n < 3:
                    slot, use = idx_slot(n + 2)
                    split_hi(slot, use, 1 if n == 2 else None, KT * IK_COLS if n == 2 else 1024)
                else:
                    split_hi(n - 3, 1, n - 3 + 2)
                if n in (0, 3):
                    sines(0 if n == 0 else 2)
                    sines(1 if n == 0 else 3)
                    nc.scalar.preload_act_table_set("natural_log_exp_and_others")
            sc.wait_ge(ikc_ok, 1)
            sc.activation(relu[0][0:IDX_DIM, :], r_tmp[0:IDX_DIM, :], ACT.Square).then_inc(iksq_ok, 1)
            sc.wait_ge(ikv_mm, 1)
            sc.activation(relu[1][0:IDX_DIM, :], ps[6][0:IDX_DIM, :], ACT.Ln, scale=1.0 / IDX_DIM,
                          bias=eps[0:IDX_DIM, :]).then_inc(ikln, 1)
            sc.wait_ge(ikln, 1)
            sc.activation(relu[1][0:IDX_DIM, :], relu[1][0:IDX_DIM, :], ACT.Exp, scale=-0.5).then_inc(ikr_ok, 1)
            def hg_f(hh):
                sc.wait_ge(group_done, hh * 4 + (G_HG + 1))
                if not (isinstance(hh, int) and hh == 0):
                    sc.wait_ge(raw_taken, hh)
                sc.activation(f_, ps[1][:, :], ACT.Sigmoid).then_inc(f_sig, 1)
                split_hi(2, hh + U_HG[2], hh * 4 + 4)

            def hg_q(hh):
                sc.wait_ge(group_done, hh * 4 + (G_HG + 2))
                sc.activation(q_sig, ps[0][:, :], ACT.Sigmoid)
                sc.activation(q_raw, ps[0][:, :], ACT.Copy).then_inc(q_ok, 1)
                split_hi(3, hh + U_HG[3], hh * 4 + 5)

            def hg_i(hh):
                sc.wait_ge(group_done, hh * 4 + (G_HG + 3))
                sc.activation(i_t, ps[1][:, :], ACT.Copy).then_inc(i_raw, 1)
                split_hi(0, hh + (U_HG[0] + 1), hh * 4 + 6)

            def hg_g(hh):
                sc.wait_ge(group_done, hh * 4 + (G_HG + 4))
                sc.activation(g_sig, ps[0][:, :], ACT.Sigmoid)
                sc.activation(g_raw, ps[0][:, :], ACT.Copy).then_inc(g_ok, 1)
                split_hi(1, hh + (U_HG[1] + 1), hh * 4 + 7)

            def att_raw(h):
                for j, dst in enumerate((aq, ak, av)):
                    sc.wait_ge(group_done, h * 3 + (G_ATT + j + 1))
                    sc.activation(dst, ps[(1, 0, 1)[j]][:, :], ACT.Copy).then_inc(a_raw, 1)
                    if j == 0:
                        split_hi(2, h + U_ATT[2], h * 3 + 21)
                    else:
                        split_hi(j - 1, h + (U_ATT[j - 1] + 1), h * 3 + (G_ATT + j))

            def hg_body(h, last):
                sc.wait_ge(iv_mm, h + 1)
                sc.activation(i_tok, ps[6][:, :], ACT.Copy).then_inc(iv_ok, 1)
                if last:
                    att_raw(0)
                else:
                    hg_f(h + 1)
                    hg_q(h + 1)
                    hg_i(h + 1)
                    hg_g(h + 1)
                nc.scalar.preload_act_table_set("natural_log_exp_and_others")
                sc.wait_ge(o_mm, h + 1)
                sc.activation(o_sq, ps[7][:, :], ACT.Square).then_inc(osq_ok, 1)
                sc.wait_ge(oss_mm, h + 1)
                sc.activation(o_rstd, ps[4][:, :], ACT.Ln, scale=1.0 / HEAD, bias=eps[:, :]).then_inc(oln_ok, 1)
                sc.wait_ge(oln_ok, h + 1)
                sc.activation(o_rstd, o_rstd, ACT.Exp, scale=-0.5).then_inc(ors_ok, 1)

            sc.wait_ge(wt_mm, 1)
            sc.activation(w_tok[:, :], ps[7][:, 0:IDX_HEADS * TT], ACT.Copy,
                          scale=float(IDX_HEADS ** -0.5 * IDX_DIM ** -0.5)).then_inc(wt_ok, 1)
            hg_f(0)
            hg_q(0)
            sc.wait_ge(ikd_mm, 1)
            sc.activation(ik, ps[6][:, :], ACT.Copy).then_inc(ik_ok, 1)
            hg_i(0)
            hg_g(0)
            n = 0
            for t in range(1, TT):
                for h in range(IDX_HEADS):
                    sc.wait_ge(sc_mm, n + 1)
                    if n >= 2:
                        sc.wait_ge(sc_acc, n - 1)
                    sc.activation(relu[n % 2][:, 0:P * (t + 1)], ps[2 + n % 4][:, 0:P * (t + 1)],
                                  ACT.Relu).then_inc(sc_relu, 1)
                    n += 1

            with sc.Fori(0, HG_HEADS - 1) as h:
                hg_body(h, False)
            hg_body(HG_HEADS - 1, True)

            for n in range(4):
                sc.wait_ge(gate_mm, 4 * n + 4)
                sc.activation((gate_mix if n < 2 else gate_ffn)[:, (n % 2) * SEQ:(n % 2 + 1) * SEQ], ps[2 + n][:, :],
                              ACT.Copy).then_inc(gate_ok, 1)

            def split_x_hi(k):
                sc.activation(h_hi[:, k * SEQ:(k + 1) * SEQ], mix[:, k * SEQ:(k + 1) * SEQ], ACT.Copy).then_inc(xs_hi, 1)

            def att_body(h, last):
                sc.wait_ge(v_mm, h + 1)
                sc.activation(av_tok, ps[6][:, :], ACT.Copy).then_inc(v_ok, 1)

                def put_pt(t):
                    sc.wait_ge(pt_mm, h * 4 + (t + 1))
                    sc.activation(pt.rearrange("p (s t) -> p s t", s=TT)[:, 0:t + 1, t * P:(t + 1) * P],
                                  ps[4 + t % 2][:, 0:P * (t + 1)].rearrange("p (s t) -> p s t", s=t + 1),
                                  ACT.Copy).then_inc(pt_ok, 1)

                for t in range(TT):
                    sc.wait_ge(nm_ok, h * 4 + (t + 1))
                    sc.activation(probs[t], probs[t], ACT.Exp, bias=nmx[:, t:t + 1], scale=float(HEAD ** -0.5),
                                  accum_out=rs[:, t:t + 1]).then_inc(exp_ok, 1)
                    if t >= 2:
                        put_pt(t - 2)
                    if last:
                        split_x_hi(t)
                        if t < 2:
                            split_hi(2 + t, U_OUT[2 + t], G_OUT)
                put_pt(2)
                put_pt(3)

            att_body(0, False)
            with sc.Fori(1, ATT_HEADS - 1) as h:
                att_raw(h)
                att_body(h, False)
            att_raw(ATT_HEADS - 1)
            sc.wait_ge(att_out, ATT_HEADS - 1)
            att_body(ATT_HEADS - 1, True)
            for k in range(4, KT):
                if k == KT - 1:
                    sc.wait_ge(att_out, ATT_HEADS)
                split_x_hi(k)

            def y_stats(seen, t):
                if t < TT - 1:
                    sc.wait_ge(tile_done, (TT - 1) * seen + t + 1)
                else:
                    sc.wait_ge(group_done, (G_FIN, N_GROUPS)[seen])
                for b in (2 * t, 2 * t + 1):
                    if b >= 2 or seen:
                        sc.wait_ge(ysq_ok, 8 * seen + b - 1)
                    if seen or t >= 2:
                        sc.wait_ge(ss_ok, TT + (TT if seen else t - 1))
                    sc.activation(junk[:, (b % 2) * SEQ:(b % 2 + 1) * SEQ], ps[b][:, :], ACT.Square,
                                  accum_out=ss[:, 8 + b:9 + b]).then_inc(ysq_ok, 1)
                n = TT * seen + t
                sc.wait_ge(ysq_ok, 2 * n + 2)
                sc.activation(ss[:, 4 + t:5 + t], ss[:, 8 + 2 * t:9 + 2 * t], ACT.Identity, scale=1.0 / D_MODEL,
                              bias=eps[:, :]).then_inc(yb_ok, 1)
                sc.wait_ge(yb_ok, n + 1)
                sc.activation(rstd[:, 4 + t:5 + t], ss[:, 9 + 2 * t:10 + 2 * t], ACT.Ln, scale=1.0 / D_MODEL,
                              bias=ss[:, 4 + t:5 + t]).then_inc(yln_ok, 1)
                sc.wait_ge(yln_ok, n + 1)
                sc.activation(rstd[:, 4 + t:5 + t], rstd[:, 4 + t:5 + t], ACT.Exp, scale=-0.5).then_inc(yrs_ok, 1)

            for k in range(4, KT):
                split_hi(k % 4, U_OUT[k % 4] + 1, G_OUT + k - 3)
            for t in range(TT):
                y_stats(0, t)
                if t == 0:
                    continue
                row_stats(1, t - 1)
            split_hi(0, U_FIN[0], G_FIN - 3)
            row_stats(1, TT - 1)
            split_hi(1, U_FIN[1], G_FIN - 2)
            norm_hi(1, 24, scale_ffn)
            with sc.Fori(0, FT // 2) as i:
                for u in range(4):
                    if u % 2 == 0:
                        sc.wait_ge(group_done, i * 4 + (G_FIN + u + 1))
                        sc.activation(silu_g[u // 2], ps[u][:, :], ACT.Silu).then_inc(silu_done[u // 2], 1)
                    if u < 2:
                        split_hi(u + 2, i + U_FIN[u + 2], i * 4 + (G_FIN + u - 1))
                    else:
                        split_hi(u - 2, i + (U_FIN[u - 2] + 1), i * 4 + (G_FIN + u - 1))
            nc.scalar.preload_act_table_set("natural_log_exp_and_others")
            with sc.Fori(0, FT // 4) as i:
                for n, slot in enumerate((2, 3, 0, 1)):
                    split_hi(slot, i + (U_FOUT[slot] + n // 2), i * 4 + (G_FOUT - 1 + n))
            for t in range(TT):
                y_stats(1, t)

        @block.vector
        def _(ve):
            V = nc.vector

            def wait_apart(s, value):
                ve.wait_ge(s, value)
                ve.sem_inc(ve_waits, 1)

            ve.wait_ge(prm_mm, 1)
            V.tensor_copy(prm[:, :], ps[6][:, 0:N_PRM]).then_inc(prm_ok, 1)
            ve.wait_ge(prm_ok, 1)
            V.tensor_tensor(lb_diff[:, :], prm[:, C_LB:C_LB + 4], prm[:, C_LB + 4:C_LB + 8],
                            ALU.subtract).then_inc(lbd_ok, 1)
            hpv = hg_par[:, :].rearrange("p (h n) -> p h n", n=3)
            V.tensor_copy(hpv[:, :, 2], prm[:, C_ONORM:C_ONORM + 4])
            ve.wait_ge(lb_ok, 1)
            V.tensor_scalar(hpv[:, :, 0], hpv[:, :, 1], -1.0, 1.0, ALU.mult, ALU.add).then_inc(small, 1)

            two_pi = 2 * np.pi
            c1 = float(np.float32(6.28125))
            c2 = float(np.float32(np.round((two_pi - c1) * 2 ** 20) / 2 ** 20))
            c3 = float(np.float32(two_pi - c1 - c2))
            steps = [0]

            def astep(ins):
                steps[0] += 1
                ins.then_inc(ang_step, 1)
                ve.wait_ge(ang_step, steps[0])

            def norm_rows(seen, t):
                ve.wait_ge(rstd_ok, TT * seen + t + 1)
                V.tensor_scalar(xn[:, t * D_MODEL:(t + 1) * D_MODEL], xr[:, t * D_MODEL:(t + 1) * D_MODEL],
                                rstd[:, t:t + 1], None, ALU.mult).then_inc(xn_ok, 1)

            for t in range(TT):
                norm_rows(0, t)

            def angles(kind, second_half):
                a, turns = ang[2 * kind + 1], ang[2 * kind]
                if not second_half:
                    astep(V.tensor_scalar(a, pos, rc[:, 2 * kind:2 * kind + 1], None, ALU.mult))
                    astep(V.tensor_scalar(turns, a, float(1 / two_pi), None, ALU.mult))
                    astep(V.tensor_scalar(turns, turns, float(1.5 * 2 ** 23), None, ALU.add))
                    astep(V.tensor_scalar(turns, turns, float(1.5 * 2 ** 23), None, ALU.subtract))
                    for piece in (c1, c2, c3):
                        astep(V.scalar_tensor_tensor(out=a, in0=turns, scalar=-piece, in1=a, op0=ALU.mult, op1=ALU.add))
                    return
                astep(V.tensor_scalar(turns, a, float(np.pi / 2), None, ALU.add))
                astep(V.tensor_scalar(turn_fix, turns, float(np.pi), -two_pi, ALU.is_gt, ALU.mult))
                astep(V.tensor_tensor(turns, turns, turn_fix, ALU.add))
                astep(V.tensor_scalar(turns, turns, 3.1415925, -3.1415925, ALU.min, ALU.max))
                astep(V.tensor_scalar(a, a, rc[:, 2 * kind + 1:2 * kind + 2], None, ALU.mult))
                astep(V.tensor_scalar(a, a, 3.1415925, -3.1415925, ALU.min, ALU.max))

            ve.wait_ge(consts, 1)

            def norm_features(seen, shift_at, scale_cols):
                def lo(k):
                    ve.wait_ge(hhi_ok, KT * seen + k + 1)
                    V.tensor_tensor(h_lo[:, k * SEQ:(k + 1) * SEQ], h32[k % 4],
                                    h_hi[:, k * SEQ:(k + 1) * SEQ].bitcast(f32), ALU.subtract).then_inc(hlo_ok, 1)

                for k in range(0, KT, 2):
                    n = KT * seen + k
                    ve.wait_ge(xt_mm, n + 1)
                    if k >= 4:
                        ve.wait_ge(hlo_ok, n - 3)
                    V.tensor_scalar(h32[k % 4], ps[k][:, :], scale_cols[:, k:k + 1],
                                    mod[:, shift_at + k:shift_at + k + 1], ALU.mult, ALU.add).then_inc(h32_even, 1)
                    if k:
                        lo(k - 2)
                        lo(k - 1)
                lo(KT - 2)
                lo(KT - 1)

            def ada_pair(cols, dsts, counter, done):
                for k in range(KT):
                    for n, (w, dst) in enumerate(zip(cols, dsts)):
                        ck = silu_c[:, k:k + 1]
                        if k == 0:
                            ins = V.tensor_scalar(dst, w[:, 0:P], ck, None, ALU.mult)
                        else:
                            wait_apart(counter, done + (2 * k + n - 1))
                            ins = V.scalar_tensor_tensor(out=dst, in0=w[:, k * P:(k + 1) * P], scalar=ck, in1=dst,
                                                         op0=ALU.mult, op1=ALU.add)
                        ins.then_inc(counter, 1)

            ve.wait_ge(silu_ok, 1)
            for n in range(0, len(ADA_ON_VE), 2):
                pair = ADA_ON_VE[n:n + 2]
                for c in pair:
                    ve.wait_ge(start_loaded[c], 16)
                cols = [start_slot[c % len(start_slot)] for c in pair]
                ada_pair(cols, [w[:, 0:P] for w in cols], ada_start, n * KT)

            ve.wait_ge(ada_used, START_ADA)
            V.tensor_tensor(mod[:, 0:16], ps[7][:, 0:16], prm[:, 0:16], ALU.add).then_inc(mod_ok, 1)
            ve.wait_ge(mod_ok, 1)
            V.scalar_tensor_tensor(out=scale_mix[:, :], in0=mod[:, 8:16], scalar=1.0,
                                   in1=prm[:, C_PRE_MIX:C_PRE_MIX + KT], op0=ALU.add,
                                   op1=ALU.mult).then_inc(scale_ok, 1)
            ve.wait_ge(scale_ok, 1)
            norm_features(0, 0, scale_mix)

            ve.wait_ge(pos_loaded, 64)
            astep(V.tensor_copy(pos, pos_i[:, :].bitcast(i32)))
            angles(1, False)
            angles(1, True)
            ve.wait_ge(sin_ok, 2)

            def rotate(dst, partner, cos, sin, n, t1, t2):
                V.tensor_tensor(t1, dst, cos, ALU.mult)
                V.tensor_tensor(t2, partner, sin, ALU.mult).then_inc(idx_t, 1)
                ve.wait_ge(idx_t, n + 1)
                V.tensor_tensor(dst, t1, t2, ALU.add).then_inc(idx_ok, 1)

            for n in range(4):
                ve.wait_ge(idx_swap, n + 1)
                if n:
                    ve.wait_ge(idx_ok, n)
                rotate(iq[:, n * SEQ:(n + 1) * SEQ], ps[6][:, :], cos_i, sin_i, n, r_tmp, r_tmp2)
                if n < 2:
                    angles(0, n == 1)
            kd = slice(0, IDX_DIM)
            ve.wait_ge(ikm_mm, 1)
            ve.wait_ge(idx_ok, 4)
            V.scalar_tensor_tensor(out=r_tmp[kd, :], in0=ps[6][kd, :], scalar=-1.0 / IDX_DIM, in1=ikw[kd, :],
                                   op0=ALU.mult, op1=ALU.add).then_inc(ikc_ok, 1)
            ve.wait_ge(ikr_ok, 1)
            ve.wait_ge(ikc_ok, 1)
            V.tensor_tensor(r_tmp[kd, :], r_tmp[kd, :], relu[1][kd, :], ALU.mult).then_inc(ikn_step, 1)
            ve.wait_ge(ikn_step, 1)
            V.tensor_scalar(r_tmp[kd, :], r_tmp[kd, :], knorm[kd, 0:1], knorm[kd, 1:2], ALU.mult,
                            ALU.add).then_inc(ikn_ok, 1)
            ve.wait_ge(idx_swap, 5)
            ve.wait_ge(ikn_ok, 1)
            rotate(r_tmp[kd, :], ps[6][kd, :], cos_i[kd, :], sin_i[kd, :], 4, r_tmp2[kd, :], relu[0][kd, :])

            ve.wait_ge(wt_ok, 1)
            n = 0
            for t in range(1, TT):
                for h in range(IDX_HEADS):
                    ve.wait_ge(sc_relu, n + 1)
                    w = w_tok[:, t * IDX_HEADS + h:t * IDX_HEADS + h + 1]
                    r = relu[n % 2][:, 0:P * (t + 1)]
                    if h == 0:
                        V.tensor_scalar(sc_t[t], r, w, None, ALU.mult).then_inc(sc_acc, 1)
                    else:
                        ve.wait_ge(sc_acc, n)
                        V.scalar_tensor_tensor(out=sc_t[t], in0=r, scalar=w, in1=sc_t[t], op0=ALU.mult,
                                               op1=ALU.add).then_inc(sc_acc, 1)
                    n += 1
                ve.wait_ge(sc_acc, n)
                V.tensor_tensor(sc_t[t][:, t * P:(t + 1) * P], sc_t[t][:, t * P:(t + 1) * P], bias_t[0],
                                ALU.add).then_inc(causal_ok, 1)
            ve.wait_ge(causal_ok, TT - 1)

            with ve.Fori(0, HG_HEADS) as h:
                def top_round(r, t):
                    n = h * 12 + (3 * r + t)
                    V.max(top8[:, 8 * (t - 1):8 * t], sc_t[t]).then_inc(top_max, 1)
                    wait_apart(top_max, n)
                    V.match_replace(out=sc_t[t], in_to_replace=top8[:, 8 * (t - 1):8 * t], in_values=sc_t[t],
                                    imm_value=TAKEN).then_inc(top_rep, 1)
                    wait_apart(top_rep, n)

                V.tensor_copy(hp[:, :], hg_par[:, ds(h * 3, 3)]).then_inc(hp_ok, 1)
                ve.wait_ge(f_sig, h + 1)
                ve.wait_ge(hp_ok, h + 1)
                V.tensor_scalar(f_w, f_, hp[:, 0:1], hp[:, 1:2], ALU.mult, ALU.add).then_inc(f_ok, 1)
                ve.wait_ge(f_ok, h + 1)
                V.tensor_scalar(k_b, f_w, -1.0, 1.0, ALU.mult, ALU.add)
                ve.wait_ge(q_ok, h + 1)
                V.scalar_tensor_tensor(out=q_f, in0=q_raw, scalar=float(HEAD ** -0.5), in1=q_sig, op0=ALU.mult,
                                       op1=ALU.mult).then_inc(lvl_ready, 1)
                ve.wait_ge(g_ok, h + 1)
                V.tensor_tensor(g_w, g_raw, g_sig, ALU.mult).then_inc(raw_taken, 1)
                t_off = 0
                src = f_w
                for st in range(LEVELS):
                    half = 0 if st == 0 else 1 << (st - 1)
                    ve.wait_ge(lvl_mm, h * LEVELS + (st + 1))
                    if st == 0:
                        V.tensor_tensor(q_f, q_f, f_w, ALU.mult).then_inc(lvl_ready, 1)
                    elif st < LEVELS - 1:
                        nb = SEQ // (2 * half)
                        qv = q_f.rearrange("p (b two h) -> p b two h", two=2, h=half)
                        kv = k_b.rearrange("p (b two h) -> p b two h", two=2, h=half)
                        tv = src.rearrange("p (b two) -> p b two", two=2)
                        if st > 1:
                            ve.wait_ge(tot_ok, h * 8 + (st - 1))
                        V.tensor_tensor(qv[:, :, 1, :], qv[:, :, 1, :],
                                        tv[:, :, 0:1].to_broadcast([P, nb, half]), ALU.mult)
                        V.tensor_tensor(kv[:, :, 0, :], kv[:, :, 0, :],
                                        tv[:, :, 1:2].to_broadcast([P, nb, half]), ALU.mult).then_inc(lvl_ready, 1)
                        nxt = tot[:, t_off:t_off + nb]
                        V.tensor_tensor(nxt, tv[:, :, 0], tv[:, :, 1], ALU.mult).then_inc(tot_ok, 1)
                        src, t_off = nxt, t_off + nb
                    pv = ps[2 + st % 2][:, :].rearrange("p (c t) -> p c t", c=TT)
                    if st == 0:
                        V.tensor_tensor(at_diag, pv, ident[:, None, :].to_broadcast([P, TT, P]),
                                        ALU.mult).then_inc(lvl_out, 1)
                    elif st < 8:
                        m = masks[:, None, (st - 1) * P:st * P].bitcast(u32).to_broadcast([P, TT, P])
                        wait_apart(lvl_out, h * LEVELS + st)
                        V.copy_predicated(at_diag, m, pv).then_inc(lvl_out, 1)
                    elif st == 8:
                        V.tensor_copy(att_hg[:, P:2 * P], ps[2][:, 0:P])
                        V.tensor_copy(att_hg[:, 2 * SEQ + 3 * P:3 * SEQ], ps[2][:, P:2 * P]).then_inc(lvl_out, 1)
                    else:
                        V.tensor_copy(att_hg[:, 0:2 * SEQ].rearrange("p (c t) -> p c t", c=2)[:, :, 2 * P:4 * P],
                                      ps[3][:, :].rearrange("p (c t) -> p c t", c=2)).then_inc(lvl_out, 1)
                    if st == 2:
                        ve.wait_ge(ada_sum, h + 1)
                        V.tensor_tensor(mod[:, ds(h * 2 + 16, 2)], ps[5][:, 0:2], prm[:, ds(h * 2 + 16, 2)], ALU.add)
                        V.tensor_tensor(mod[:, ds(h * 2 + 40, 2)], ps[5][:, 2:4], prm[:, ds(h * 2 + 40, 2)],
                                        ALU.add).then_inc(mod_ok, 1)
                    for n in ((0, 1), (2,), (3,), (4,), (5,), (6,), (7,), (8,), (), (9, 10, 11))[st]:
                        top_round(n // 3, n % 3 + 1)
                ve.wait_ge(ors_ok, h + 1)
                V.tensor_tensor(o_n, ps[7][:, :], o_rstd, ALU.mult).then_inc(on_ok, 1)
                ve.wait_ge(on_ok, h + 1)
                V.scalar_tensor_tensor(out=mix[:, ds(h * SEQ, SEQ)], in0=o_n, scalar=hp[:, 2:3], in1=g_w,
                                       op0=ALU.mult, op1=ALU.mult).then_inc(hg_out, 1)
                ve.wait_ge(hg_out, h + 1)

            for t in range(1, TT):
                V.tensor_scalar(bias_t[t], sc_t[t], TAKEN / 2, NEG, ALU.is_gt, ALU.mult).then_inc(bias_ok, 1)
            ve.wait_ge(bias_ok, TT - 1)
            ve.wait_ge(mod_ok, 5)
            V.tensor_tensor(gate_cols[:, 0:KT], mod[:, 16:24], prm[:, C_POST_MIX:C_POST_MIX + KT], ALU.mult)
            V.tensor_tensor(gate_cols[:, KT:2 * KT], mod[:, 40:48], prm[:, C_POST_FFN:C_POST_FFN + KT],
                            ALU.mult).then_inc(gc_ok, 1)
            ve.wait_ge(gc_ok, 1)
            ve.wait_ge(hg_out, HG_HEADS)
            for n in range(2 * KT):
                V.tensor_scalar(diag[:, n * P:(n + 1) * P], ident[:, :], gate_cols[:, n:n + 1], None,
                                ALU.mult).then_inc(diag_ok, 1)

            def late_ada(h, pair):
                for c in range(2):
                    wait_apart(ada_loaded[c], h * 32 + (HG_HEADS * 32 + 16 * pair + 16))
                ada_pair([adaw[c] for c in range(2)], [ada_part[:, (2 * pair + c) * P:(2 * pair + c + 1) * P]
                                                       for c in range(2)], ada_late, h * 32 + 16 * pair)

            def att_body(h):
                late_ada(h, 0)
                rot = slice(0, 32)
                for n, dst in enumerate((aq, ak)):
                    ve.wait_ge(a_swap, h * 2 + (n + 1))
                    if n:
                        ve.wait_ge(a_rope, h * 2 + n)
                    V.tensor_tensor(o_sq[rot, :], dst[rot, :], cos_h[rot, :], ALU.mult)
                    V.tensor_tensor(o_rstd[rot, :], ps[6][rot, :], sin_h[rot, :], ALU.mult).then_inc(a_t, 1)
                    ve.wait_ge(a_t, h * 2 + (n + 1))
                    V.tensor_tensor(dst[rot, :], o_sq[rot, :], o_rstd[rot, :], ALU.add).then_inc(a_rope, 1)

                def normalise(t):
                    ve.wait_ge(exp_ok, h * 4 + (t + 1))
                    V.reciprocal(ri[:, t:t + 1], rs[:, t:t + 1]).then_inc(ri_ok, 1)
                    ve.wait_ge(ri_ok, h * 4 + (t + 1))
                    V.tensor_scalar(probs[t], probs[t], ri[:, t:t + 1], None, ALU.mult).then_inc(p_ok, 1)

                for t in range(TT):
                    wait_apart(lg_mm, h * 4 + (t + 1))
                    V.tensor_tensor_reduce(out=probs[t], in0=ps[2 + t % 2][:, 0:P * (t + 1)], in1=bias_t[t], scale=1.0,
                                           scalar=TAKEN, op0=ALU.add, op1=ALU.max,
                                           accum_out=mx[:, t:t + 1]).then_inc(lg_ok, 1)
                    ve.wait_ge(lg_ok, h * 4 + (t + 1))
                    V.tensor_scalar(nmx[:, t:t + 1], mx[:, t:t + 1], float(-HEAD ** -0.5), None,
                                    ALU.mult).then_inc(nm_ok, 1)
                    if t:
                        normalise(t - 1)
                normalise(TT - 1)
                late_ada(h, 1)
                ve.wait_ge(pv_mm, h * 4 + 4)
                V.tensor_copy(mix[:, ds(h * SEQ + HG_HEADS * SEQ, SEQ)], ps[7][:, :]).then_inc(att_out, 1)

                ve.wait_ge(ada_sum, h + (HG_HEADS + 1))
                V.tensor_tensor(mod[:, ds(h * 4 + 24, 4)], ps[5][:, 0:4], prm[:, ds(h * 4 + 24, 4)],
                                ALU.add).then_inc(mod_ok, 1)

            with ve.Fori(0, ATT_HEADS) as h:
                att_body(h)
            ve.wait_ge(mod_ok, 1 + HG_HEADS + ATT_HEADS)
            V.scalar_tensor_tensor(out=scale_ffn[:, :], in0=mod[:, 32:40], scalar=1.0,
                                   in1=prm[:, C_PRE_FFN:C_PRE_FFN + KT], op0=ALU.add, op1=ALU.mult).then_inc(scale_ok, 1)

            def post_norm(seen, t, gate):
                ve.wait_ge(yrs_ok, TT * seen + t + 1)
                for b in (2 * t, 2 * t + 1):
                    n = 8 * seen + b
                    if n >= 2:
                        ve.wait_ge(res_ok, n - 1)
                    V.scalar_tensor_tensor(out=y_tmp[b % 2], in0=ps[b][:, :], scalar=rstd[:, 4 + t:5 + t],
                                           in1=gate[:, (b % 2) * SEQ:(b % 2 + 1) * SEQ], op0=ALU.mult,
                                           op1=ALU.mult).then_inc(yt_ok, 1)
                for b in (2 * t, 2 * t + 1):
                    ve.wait_ge(yt_ok, 8 * seen + b + 1)
                    V.tensor_tensor(xr[:, b * SEQ:(b + 1) * SEQ], xr[:, b * SEQ:(b + 1) * SEQ], y_tmp[b % 2],
                                    ALU.add).then_inc(res_ok, 1)

            ve.wait_ge(x_again, 16 * TT)
            ve.wait_ge(gate_ok, 4)
            for t in range(TT):
                post_norm(0, t, gate_mix)
                if t:
                    norm_rows(1, t - 1)
            norm_rows(1, TT - 1)
            ve.wait_ge(scale_ok, 2)
            norm_features(1, 24, scale_ffn)
            with ve.Fori(0, FT // 2) as i:
                for v in range(2):
                    ve.wait_ge(silu_done[v], i + 1)
                    ve.wait_ge(group_done, i * 4 + (G_FIN + 2 * v + 2))
                    V.tensor_tensor(act[:, ds(i * 2 * SEQ + v * SEQ, SEQ)], silu_g[v], ps[2 * v + 1][:, :],
                                    ALU.mult).then_inc(act_ok[v], 1)

            def split_act(k, slot):
                at = slice(slot * SEQ, (slot + 1) * SEQ)
                ve.wait_ge(group_done, k + (G_FOUT - 3))
                V.tensor_copy(h_hi[:, at], act[:, ds(k * SEQ, SEQ)]).then_inc(xs_hi, 1)
                ve.wait_ge(xs_hi, k + (KT + 1))
                V.tensor_tensor(h_lo[:, at], act[:, ds(k * SEQ, SEQ)], h_hi[:, at].bitcast(f32),
                                ALU.subtract).then_inc(xs_ok, 1)

            for v in range(2):
                ve.wait_ge(act_ok[v], FT // 2)
            ve.wait_ge(group_done, G_FOUT)
            with ve.Fori(0, FT // 4) as i:
                for u in range(4):
                    split_act(i * 4 + u, u)
            for k in range(FT // 4 * 4, FT):
                split_act(k, k % 4)
            for t in range(TT):
                post_norm(1, t, gate_ffn)

        @block.tensor
        def _(te):
            mm = nc.tensor.matmul

            def feature_step(k, slot, bank, rows=P):
                wh = w_hi[slot][:, k * rows:(k + 1) * rows]
                wl = w_lo[slot][:, k * rows:(k + 1) * rows]
                hh, hl = h_hi[:, k * SEQ:(k + 1) * SEQ], h_lo[:, k * SEQ:(k + 1) * SEQ]
                for n, (a, b) in enumerate(((wh, hh), (wh, hl), (wl, hh))):
                    last = mm(ps[bank][0:rows, :], a, b, start=(k == 0 and n == 0), stop=(k == KT - 1 and n == 2))
                if k == KT - 1:
                    last.then_inc(group_done, 1)

            def feature_group(g, slot, bank, rows=P, h_count=None):
                te.wait_ge(lo_ok, g + 1)
                for k in range(KT):
                    if h_count is not None:
                        te.wait_ge(hlo_ok, h_count + k + 1)
                    feature_step(k, slot, bank, rows)

            def row_tile(slot, x_slot, t, first=False, last_one=False):
                at = x_slot * SEQ + t * P
                xh, xl = h_hi[:, at:at + P], h_lo[:, at:at + P]
                for b in range(2):
                    wh, wl = (w[slot][:, b * SEQ:(b + 1) * SEQ] for w in (w_hi, w_lo))
                    for n, (a, w) in enumerate(((xh, wh), (xh, wl), (xl, wh))):
                        last = mm(ps[2 * t + b][:, :], a, w, start=(first and n == 0), stop=(last_one and n == 2))
                return last

            def row_group(g, slot, x_slot, count, first=False):
                te.wait_ge(lo_ok, g + 1)
                te.wait_ge(xs_ok, count)
                for t in range(TT):
                    last = row_tile(slot, x_slot, t, first)
                last.then_inc(group_done, 1)

            def last_rows(g0, slots, x_slots, count):
                for t in range(TT):
                    for n in range(4):
                        if t == 0:
                            te.wait_ge(lo_ok, g0 + n + 1)
                            te.wait_ge(xs_ok, count + n + 1)
                        last = row_tile(slots[n], x_slots[n], t, last_one=(n == 3))
                        if t == TT - 1:
                            last.then_inc(group_done, 1)
                        elif n == 3:
                            last.then_inc(tile_done, 1)

            te.wait_ge(prm_loaded, 16 * 8)
            te.wait_ge(const_step, 3)
            nc.tensor.transpose(ps[6][:, 0:N_PRM], prm_rows[0:N_PRM, :], ident[0:N_PRM, 0:N_PRM]).then_inc(prm_mm, 1)
            te.wait_ge(silu_ok, 1)

            def transpose_tile(k, t):
                return nc.tensor.transpose(ps[k][:, t * P:(t + 1) * P],
                                           xn[:, t * D_MODEL + k * P:t * D_MODEL + (k + 1) * P], ident[:, :])

            own = [n for n in range(START_ADA) if n not in ADA_ON_VE and n not in ADA_ON_POOL]
            for i, n in enumerate(own + sorted(ADA_ON_VE + ADA_ON_POOL)):
                if i == len(own):
                    te.wait_ge(prm_ok, 1)
                    te.wait_ge(xn_ok, TT)
                    for k in range(KT - 1):
                        for t in range(TT):
                            last = transpose_tile(k, t)
                        last.then_inc(xt_mm, 1)
                if i >= len(own):
                    if n in ADA_ON_VE:
                        te.wait_ge(ada_start, (ADA_ON_VE.index(n) // 2 + 1) * 2 * KT)
                    else:
                        te.wait_ge(ada_first, (ADA_ON_POOL.index(n) + 1) * 4)
                    mm(ps[7][:, n:n + 1], start_slot[n % len(start_slot)][:, 0:P], ones[:, 0:1], start=True,
                       stop=True).then_inc(ada_used, 1)
                    continue
                te.wait_ge(start_loaded[n], 16)
                for k in range(KT):
                    last = mm(ps[7][:, n:n + 1], start_slot[n % len(start_slot)][:, k * P:(k + 1) * P], silu_c[:, k:k + 1],
                              start=(k == 0), stop=(k == KT - 1))
                last.then_inc(ada_used, 1)
            te.wait_ge(mod_ok, 1)
            for t in range(TT):
                last = transpose_tile(KT - 1, t)
            last.then_inc(xt_mm, 1)

            def idx_partner(n):
                te.wait_ge(acc_free[n % 2], n // 2 + 1)
                if n:
                    te.wait_ge(idx_ok, n)
                mm(ps[6][:, :], swap_idx[:, :], iq[:, n * SEQ:(n + 1) * SEQ], start=True,
                   stop=True).then_inc(idx_swap, 1)

            for n in range(5):
                if n >= 2:
                    te.wait_ge(acc_free[n % 2], n // 2)
                feature_group(n, idx_slot(n)[0], n % 2, IK_COLS if n == 4 else P, 0 if n == 0 else None)
                if n:
                    idx_partner(n - 1)
            def hg_project(hh, start, end):
                for j, k in ((s // KT, s % KT) for s in range(start, end)):
                    if k == 0:
                        te.wait_ge(lo_ok, hh * 4 + (G_HG + j + 1))
                        if j >= 2:
                            te.wait_ge((f_sig, q_ok)[j - 2], hh + 1)
                        elif isinstance(hh, int) and hh == 0:
                            te.wait_ge(acc_free[1 - j], 2 + j)
                        else:
                            te.wait_ge((i_raw, g_ok)[j], hh)
                    feature_step(k, j, 1 - j % 2)

            def att_project(h, start, end):
                for j, k in ((s // KT, s % KT) for s in range(start, end)):
                    if k == 0:
                        te.wait_ge(lo_ok, h * 3 + (G_ATT + j + 1))
                        if isinstance(h, int) and h == 0:
                            te.wait_ge((i_raw, g_ok, a_raw)[j], (HG_HEADS, HG_HEADS, 1)[j])
                        elif j == 2:
                            te.wait_ge(a_raw, h * 3 + 1)
                    feature_step(k, j, 1 - j % 2)

            def ada_sums():
                for c in range(4):
                    last = mm(ps[5][:, c:c + 1], ada_part[:, c * P:(c + 1) * P], ones[:, 0:1], start=True, stop=True)
                last.then_inc(ada_sum, 1)

            kd = slice(0, IDX_DIM)
            te.wait_ge(acc_free[0], 3)
            for t in range(TT):
                last = mm(ps[7][:, t * IDX_HEADS:(t + 1) * IDX_HEADS], ikw[IDX_DIM:IK_COLS, t * P:(t + 1) * P],
                          ident[IDX_DIM:IK_COLS, IDX_DIM:IK_COLS], start=True, stop=True)
            last.then_inc(wt_mm, 1)
            te.wait_ge(idx_ok, 4)
            mm(ps[6][kd, :], ones[kd, kd], ikw[kd, :], start=True, stop=True).then_inc(ikm_mm, 1)
            hg_project(0, 0, 8)
            te.wait_ge(iksq_ok, 1)
            te.wait_ge(ikc_ok, 1)
            mm(ps[6][kd, :], ones[kd, kd], relu[0][kd, :], start=True, stop=True).then_inc(ikv_mm, 1)
            hg_project(0, 8, 16)
            te.wait_ge(ikn_ok, 1)
            mm(ps[6][kd, :], swap_idx[kd, kd], r_tmp[kd, :], start=True, stop=True).then_inc(idx_swap, 1)
            hg_project(0, 16, 20)
            te.wait_ge(idx_ok, 5)
            mm(ps[6][:, :], dup[kd, :], r_tmp[kd, :], start=True, stop=True).then_inc(ikd_mm, 1)
            hg_project(0, 20, 32)
            te.wait_ge(ik_ok, 1)
            n = 0
            for t in range(1, TT):
                for h in range(IDX_HEADS):
                    rows = slice(IDX_DIM * (h % 2), IDX_DIM * (h % 2) + IDX_DIM)
                    if n >= 4:
                        te.wait_ge(sc_relu, n - 3)
                    mm(ps[2 + n % 4][:, 0:P * (t + 1)], iq[rows, (h // 2) * SEQ + t * P:(h // 2) * SEQ + (t + 1) * P],
                       ik[rows, 0:P * (t + 1)], start=True, stop=True).then_inc(sc_mm, 1)
                    n += 1

            te.wait_ge(sc_relu, 24)
            def hg_body(h, last_head):
                def level(st):
                    te.wait_ge(lvl_ready, h * LEVELS + (st + 1))
                    if st >= 2:
                        te.wait_ge(lvl_out, h * LEVELS + (st - 1))
                    bank = ps[2 + st % 2]
                    if st < 8:
                        for t in range(TT):
                            tt = slice(t * P, (t + 1) * P)
                            last = mm(bank[:, tt], k_b[:, tt], q_f[:, tt], start=True, stop=True)
                    elif st == 8:
                        for b in range(2):
                            last = mm(bank[:, b * P:(b + 1) * P], k_b[:, 2 * b * P:(2 * b + 1) * P],
                                      q_f[:, (2 * b + 1) * P:(2 * b + 2) * P], start=True, stop=True)
                    else:
                        for b in range(2):
                            last = mm(bank[:, b * 2 * P:(b + 1) * 2 * P], k_b[:, b * P:(b + 1) * P],
                                      q_f[:, 2 * P:4 * P], start=True, stop=True)
                    last.then_inc(lvl_mm, 1)

                def project(n):
                    if last_head:
                        att_project(0, n * 24 // 32, (n + 3 if n < 27 else n + 2) * 24 // 32)
                    else:
                        hg_project(h + 1, n, n + 3 if n < 27 else n + 2)

                te.wait_ge(i_raw, h + 1)
                for t in range(TT):
                    last = nc.tensor.transpose(ps[6][:, t * P:(t + 1) * P], i_t[:, t * P:(t + 1) * P], ident[:, :])
                last.then_inc(iv_mm, 1)
                project(0)
                for st in range(8):
                    level(st)
                    if st == 0:
                        te.wait_ge(ada_step, h * 16 + 16)
                        ada_sums()
                    project(3 + 3 * st)
                level(8)
                project(27)
                level(9)
                project(29)
                te.wait_ge(iv_ok, h + 1)
                te.wait_ge(lvl_out, h * LEVELS + LEVELS)
                for s in range(TT):
                    last = mm(ps[7][:, s * P:SEQ], i_tok[:, s * P:(s + 1) * P], att_hg[:, s * SEQ + s * P:(s + 1) * SEQ],
                              start=(s == 0), stop=(s == TT - 1))
                last.then_inc(o_mm, 1)
                if last_head:
                    att_project(0, 23, 24)
                else:
                    hg_project(h + 1, 31, 32)
                te.wait_ge(osq_ok, h + 1)
                mm(ps[4][:, :], ones[:, :], o_sq, start=True, stop=True).then_inc(oss_mm, 1)

            with te.Fori(0, HG_HEADS - 1) as h:
                hg_body(h, False)
            hg_body(HG_HEADS - 1, True)

            te.wait_ge(diag_ok, 16)
            for n in range(16):
                mm(ps[2 + n // 4][:, (n % 4) * P:(n % 4 + 1) * P], ones[:, :], diag[:, n * P:(n + 1) * P], start=True,
                   stop=True).then_inc(gate_mm, 1)

            def att_body(h):
                def partner(n, src):
                    te.wait_ge(a_raw, h * 3 + (n + 1))
                    if n:
                        te.wait_ge(a_rope, h * 2 + n)
                    te.sem_inc(te_waits, 1)
                    mm(ps[6][0:32, :], swap_head[:, :], src[0:32, :], start=True, stop=True).then_inc(a_swap, 1)

                def logits(t):
                    if t >= 2:
                        te.wait_ge(lg_ok, h * 4 + (t - 1))
                    mm(ps[2 + t % 2][:, 0:P * (t + 1)], aq[:, t * P:(t + 1) * P], ak[:, 0:P * (t + 1)], start=True,
                       stop=True).then_inc(lg_mm, 1)

                if isinstance(h, int):
                    partner(0, aq)
                    partner(1, ak)
                    te.wait_ge(gate_ok, 4)
                else:
                    att_project(h, 0, 16)
                    partner(0, aq)
                    att_project(h, 16, 20)
                    partner(1, ak)
                    att_project(h, 20, 24)
                te.wait_ge(a_rope, h * 2 + 2)
                logits(0)
                logits(1)
                te.wait_ge(a_raw, h * 3 + 3)
                for t in range(TT):
                    last = nc.tensor.transpose(ps[6][:, t * P:(t + 1) * P], av[:, t * P:(t + 1) * P], ident[:, :])
                last.then_inc(v_mm, 1)
                logits(2)
                logits(3)
                for t in range(TT):
                    te.wait_ge(p_ok, h * 4 + (t + 1))
                    if t >= 2:
                        te.wait_ge(pt_ok, h * 4 + (t - 1))
                    for s in range(t + 1):
                        last = nc.tensor.transpose(ps[4 + t % 2][:, s * P:(s + 1) * P], probs[t][:, s * P:(s + 1) * P],
                                                   ident[:, :])
                    last.then_inc(pt_mm, 1)
                te.wait_ge(v_ok, h + 1)
                for t in range(TT):
                    te.wait_ge(pt_ok, h * 4 + (t + 1))
                    for s in range(t + 1):
                        last = mm(ps[7][:, t * P:(t + 1) * P], av_tok[:, s * P:(s + 1) * P],
                                  pt[:, s * SEQ + t * P:s * SEQ + (t + 1) * P], start=(s == 0), stop=(s == t))
                    last.then_inc(pv_mm, 1)
                te.wait_ge(ada_late, h * 32 + 32)
                ada_sums()

            att_body(0)
            with te.Fori(1, ATT_HEADS) as h:
                att_body(h)

            te.wait_ge(att_out, ATT_HEADS)
            te.wait_ge(mod_ok, 1 + HG_HEADS + ATT_HEADS)
            for k in range(4):
                row_group(G_OUT + k, k, k, k + 1, k == 0)
            last_rows(G_OUT + 4, range(4), range(4, 8), 4)

            te.wait_ge(xn_ok, 2 * TT - 1)
            for k in range(KT - 2):
                for t in range(TT - 1):
                    transpose_tile(k, t)
            te.wait_ge(xn_ok, 2 * TT)
            for k in range(KT):
                for t in range(TT - 1 if k < KT - 2 else 0, TT):
                    last = transpose_tile(k, t)
                last.then_inc(xt_mm, 1)

            def fin_pass(i, first):
                for u in range(4):
                    if not first:
                        te.wait_ge(act_ok[u // 2], i)
                    feature_group(i * 4 + (G_FIN + u), u, u, h_count=KT if first and u == 0 else None)

            fin_pass(0, True)
            with te.Fori(1, FT // 2) as i:
                fin_pass(i, False)
            for v in range(2):
                te.wait_ge(act_ok[v], FT // 2)
            for k in range(4):
                row_group(G_FOUT + k, k, k, KT + k + 1, k == 0)
            full = (FT - 4) // 4
            with te.Fori(1, full) as i:
                for u in range(4):
                    row_group(i * 4 + (G_FOUT + u), u, u, i * 4 + (KT + u + 1))
            for k in range(4 * full, FT - 4):
                row_group(G_FOUT + k, k % 4, k % 4, KT + k + 1)
            last_rows(G_FOUT + FT - 4, *[[k % 4 for k in range(FT - 4, FT)]] * 2, KT + FT - 4)


_INS = ["x", "c", "positions", "w_ada", "b_ada", "norm_pre_mix", "norm_post_mix", "norm_pre_ffn", "norm_post_ffn",
        "w_in", "hgrn_lower_bound", "hgrn_out_norm", "idx_k_norm_w", "idx_k_norm_b", "w_out", "w_ffn_in", "w_ffn_out"]


def rope_constants():
    rc = np.zeros((P, 4), np.float32)
    rc[:, 1] = rc[:, 3] = 1.0
    for at, dim in ((0, HEAD), (2, IDX_DIM)):
        half = dim // 8
        freq = (np.float32(ROPE_THETA) ** (-np.arange(half, dtype=np.float32) / np.float32(half))).astype(np.float32)
        for start in range(0, P, dim):
            for j in range(half):
                rc[start + j, at:at + 2] = freq[j], -1.0
                rc[start + half + j, at:at + 2] = freq[j], 1.0
    return rc


def kernel(**inputs):
    import concourse.bacc as bacc
    from concourse.bass_utils import run_bass_kernel_spmd

    nc = bacc.Bacc("TRN2", target_bir_lowering=False, num_devices=1)
    arrays, args = {}, []
    given = {n: np.ascontiguousarray(inputs[n]) for n in _INS}
    given["rope_const"] = rope_constants()
    for name, a in given.items():
        arrays[f"in_{name}"] = a
        args.append(nc.dram_tensor(f"in_{name}", a.shape, mybir.dt.from_np(a.dtype), kind="ExternalInput").ap())
    out = nc.dram_tensor("out_0", (1, SEQ, D_MODEL), mybir.dt.float32, kind="ExternalOutput").ap()
    build(nc, *args, out)
    r = run_bass_kernel_spmd(nc, [arrays], core_ids=[0])
    return r.results[0]["out_0"]
```
